# Optimizing a Trainium2 kernel written in Bass

```python
import math
import jax, jax.numpy as jnp
from jax import lax
import numpy as np

D_MODEL = 2048
BATCH = 1
SEQ = 256
DEPTH = 2

GRID_W = 64
CTX_LEN = 256
N_MIXERS = 2
N_MLA = (DEPTH + 1) // 2
N_GDN = DEPTH // 2
EPS = 1e-6
MLA_HEADS = 16
MLA_NOPE = 128
MLA_ROPE = 64
MLA_V = 128
MLA_QK = MLA_NOPE + MLA_ROPE
Q_LORA = 512
KV_LORA = 512
MLA_WIDTH = MLA_HEADS * MLA_V
MLA_IN = Q_LORA + KV_LORA + MLA_ROPE + MLA_WIDTH
ROPE_THETA = 10000.0
Q_BLOCK = 128
GDN_K_HEADS = 16
GDN_V_HEADS = 32
GDN_DK = 128
GDN_DV = 128
GDN_KEY = GDN_K_HEADS * GDN_DK
GDN_VAL = GDN_V_HEADS * GDN_DV
GDN_CONV_CH = 2 * GDN_KEY + GDN_VAL
GDN_IN = GDN_CONV_CH + GDN_VAL + 2 * 2 * GDN_V_HEADS
CONV_W = 5
CHUNK = 64

kernel_name = "hybrid_mla_gdn_diffusion_block"

F32 = jnp.float32

def _rmsnorm(x, w):
    xf = x.astype(F32)
    y = xf * lax.rsqrt(jnp.mean(xf * xf, axis=-1, keepdims=True) + EPS)
    return (y * w.astype(F32)).astype(x.dtype)

def _l2norm(x):
    xf = x.astype(F32)
    return xf * lax.rsqrt(jnp.sum(xf * xf, axis=-1, keepdims=True) + EPS)

def _adaln(cond, w, b):
    m = jax.nn.silu(cond) @ w + b
    return jnp.split(m, 3, axis=-1)

def _axial_rope_tables(n_tokens):
    rows = n_tokens // GRID_W
    r, col = jnp.meshgrid(jnp.arange(rows), jnp.arange(GRID_W), indexing="ij")
    r = r.reshape(-1).astype(F32)
    col = col.reshape(-1).astype(F32)
    half = MLA_ROPE // 2
    inv = ROPE_THETA ** (-jnp.arange(0, half, 2, dtype=F32) / half)
    ang = jnp.concatenate([r[:, None] * inv, col[:, None] * inv], axis=-1)
    return jnp.cos(ang), jnp.sin(ang)

def _apply_rope(x, cos, sin):
    xf = x.astype(F32)
    x1, x2 = jnp.split(xf, 2, axis=-1)
    cs, sn = cos[None, :, None, :], sin[None, :, None, :]
    return jnp.concatenate([x1 * cs - x2 * sn, x1 * sn + x2 * cs], axis=-1).astype(x.dtype)

def _mla_project(h, w_in, q_norm, w_uq, kv_norm, w_ukv):
    B, T, _ = h.shape
    proj = h @ w_in
    cq, ckv, k_rope, z = jnp.split(proj, [Q_LORA, Q_LORA + KV_LORA, Q_LORA + KV_LORA + MLA_ROPE], axis=-1)
    q = (_rmsnorm(cq, q_norm) @ w_uq).reshape(B, T, MLA_HEADS, MLA_QK)
    kv = (_rmsnorm(ckv, kv_norm) @ w_ukv).reshape(B, T, MLA_HEADS, MLA_NOPE + MLA_V)
    return (q[..., :MLA_NOPE], q[..., MLA_NOPE:], kv[..., :MLA_NOPE],
            k_rope[:, :, None, :], kv[..., MLA_NOPE:], z)

def _mla_keys(k_nope, k_rope):
    return jnp.concatenate([k_nope, jnp.broadcast_to(k_rope, k_nope.shape[:-1] + (MLA_ROPE,))], axis=-1)

def _softmax_attend(q, k, v):
    s = jnp.einsum("bqhd,bkhd->bhqk", q, k, preferred_element_type=F32) * (MLA_QK ** -0.5)
    p = jax.nn.softmax(s, axis=-1).astype(v.dtype)
    return jnp.einsum("bhqk,bkhd->bqhd", p, v)

def _blocked_attend(q, k, v):
    B, S, H, Dq = q.shape
    nb = S // Q_BLOCK
    qb = jnp.moveaxis(q.reshape(B, nb, Q_BLOCK, H, Dq), 1, 0)
    ob = lax.map(lambda qq: _softmax_attend(qq, k, v), qb)
    return jnp.moveaxis(ob, 0, 1).reshape(B, S, H, v.shape[-1])

def _mla_mixer(h, h_ctx, cos, sin, w_in, q_norm, w_uq, kv_norm, w_ukv, w_o, need_ctx_out):
    B, S, _ = h.shape
    qn, qr, kn, kr, v, z = _mla_project(h, w_in, q_norm, w_uq, kv_norm, w_ukv)
    qnc, qrc, knc, krc, vc, zc = _mla_project(h_ctx, w_in, q_norm, w_uq, kv_norm, w_ukv)
    q = jnp.concatenate([qn, _apply_rope(qr, cos, sin)], axis=-1)
    k = _mla_keys(kn, _apply_rope(kr, cos, sin))
    k_c = _mla_keys(knc, krc)
    keys = jnp.concatenate([k_c, k], axis=1)
    vals = jnp.concatenate([vc, v], axis=1)
    o = _blocked_attend(q, keys, vals).reshape(B, S, MLA_WIDTH)
    y = (o * jax.nn.silu(z)) @ w_o
    y_ctx = None
    if need_ctx_out:
        q_c = jnp.concatenate([qnc, qrc], axis=-1)
        o_c = _softmax_attend(q_c, k_c, vc).reshape(B, h_ctx.shape[1], MLA_WIDTH)
        y_ctx = (o_c * jax.nn.silu(zc)) @ w_o
    return y, y_ctx

def _depthwise_conv(x, w):
    return lax.conv_general_dilated(
        x, w[:, None, :].astype(x.dtype), window_strides=(1,),
        padding=[(CONV_W // 2, CONV_W // 2)],
        dimension_numbers=("NWC", "WIO", "NWC"), feature_group_count=x.shape[-1])

def _gdn_project(h, w_in, conv_w, a_log, dt_bias):
    B, T, _ = h.shape
    proj = h @ w_in
    qkv, z, b, a = jnp.split(proj, [GDN_CONV_CH, GDN_CONV_CH + GDN_VAL,
                                    GDN_CONV_CH + GDN_VAL + 2 * GDN_V_HEADS], axis=-1)
    qkv = jax.nn.silu(_depthwise_conv(qkv, conv_w))
    q, k, v = jnp.split(qkv, [GDN_KEY, 2 * GDN_KEY], axis=-1)
    rep = GDN_V_HEADS // GDN_K_HEADS
    q = jnp.repeat(_l2norm(q.reshape(B, T, GDN_K_HEADS, GDN_DK)), rep, axis=2)
    k = jnp.repeat(_l2norm(k.reshape(B, T, GDN_K_HEADS, GDN_DK)), rep, axis=2)
    v = v.reshape(B, T, GDN_V_HEADS, GDN_DV).astype(F32)
    beta = jax.nn.sigmoid(b.reshape(B, T, 2, GDN_V_HEADS).astype(F32))
    g = -jnp.exp(a_log.astype(F32)) * jax.nn.softplus(
        a.reshape(B, T, 2, GDN_V_HEADS).astype(F32) + dt_bias.astype(F32))
    return q, k, v, g, beta, z

def _to_chunks(x):
    B, T, H = x.shape[:3]
    x = x.reshape((B, T // CHUNK, CHUNK, H) + x.shape[3:])
    return jnp.moveaxis(x, 3, 1)

def _gdn_chunked(q, k, v, g, beta, state0):
    B, T, H, _ = q.shape
    qc = _to_chunks(q * (GDN_DK ** -0.5))
    kc = _to_chunks(k)
    vc = _to_chunks(v)
    gcum = jnp.cumsum(_to_chunks(g), axis=-1)
    bc = _to_chunks(beta)
    incl = jnp.tril(jnp.ones((CHUNK, CHUNK), bool))
    strict = jnp.tril(jnp.ones((CHUNK, CHUNK), bool), -1)
    decay = jnp.exp(jnp.where(incl, gcum[..., :, None] - gcum[..., None, :], -jnp.inf))
    kb = kc * bc[..., None]
    a_mat = jnp.where(strict, jnp.einsum("bhnid,bhnjd->bhnij", kb, kc) * decay, 0.0)
    lhs = a_mat + jnp.eye(CHUNK, dtype=F32)
    rhs = jnp.concatenate([vc * bc[..., None], kb * jnp.exp(gcum)[..., None]], axis=-1)
    sol = lax.linalg.triangular_solve(lhs, rhs, left_side=True, lower=True)
    u, w = sol[..., :GDN_DV], sol[..., GDN_DV:]
    qk = jnp.einsum("bhnid,bhnjd->bhnij", qc, kc) * decay
    q_dec = qc * jnp.exp(gcum)[..., None]
    k_dec = kc * jnp.exp(gcum[..., -1:] - gcum)[..., None]
    c_dec = jnp.exp(gcum[..., -1])

    def step(state, blk):
        u_b, w_b, qk_b, qd_b, kd_b, cd_b = blk
        v_new = u_b - jnp.einsum("bhlk,bhkv->bhlv", w_b, state)
        o_b = (jnp.einsum("bhlk,bhkv->bhlv", qd_b, state)
               + jnp.einsum("bhij,bhjv->bhiv", qk_b, v_new))
        state = state * cd_b[..., None, None] + jnp.einsum("bhlk,bhlv->bhkv", kd_b, v_new)
        return state, o_b

    xs = tuple(jnp.moveaxis(t, 2, 0) for t in (u, w, qk, q_dec, k_dec, c_dec))
    state, o = lax.scan(step, state0, xs)
    o = jnp.transpose(o, (1, 0, 3, 2, 4)).reshape(B, T, H, GDN_DV)
    return o, state

def _flip(t, flip):
    return t[:, ::-1] if flip else t

def _gdn_out(o, z, o_norm, w_o):
    B, T = o.shape[:2]
    o = _rmsnorm(o, o_norm).reshape(B, T, GDN_VAL) * jax.nn.silu(z.astype(F32))
    return o.astype(w_o.dtype) @ w_o

def _gdn_mixer(h, h_ctx, w_in, conv_w, a_log, dt_bias, o_norm, w_o, need_ctx_out):
    q, k, v, g, beta, z = _gdn_project(h, w_in, conv_w, a_log, dt_bias)
    qc, kc, vc, gc, bc, zc = _gdn_project(h_ctx, w_in, conv_w, a_log, dt_bias)
    zero = jnp.zeros((h.shape[0], GDN_V_HEADS, GDN_DK, GDN_DV), F32)
    o = 0.0
    o_c = 0.0
    for d in range(2):
        fl = d == 1
        oc_d, s_ctx = _gdn_chunked(_flip(qc, fl), _flip(kc, fl), _flip(vc, fl),
                                   _flip(gc[:, :, d], fl), _flip(bc[:, :, d], fl), zero)
        o_d, _ = _gdn_chunked(_flip(q, fl), _flip(k, fl), _flip(v, fl),
                              _flip(g[:, :, d], fl), _flip(beta[:, :, d], fl), s_ctx)
        o = o + _flip(o_d, fl)
        o_c = o_c + _flip(oc_d, fl)
    y = _gdn_out(o, z, o_norm, w_o)
    y_ctx = _gdn_out(o_c, zc, o_norm, w_o) if need_ctx_out else None
    return y, y_ctx

def setup_inputs(seed: int = 0) -> dict:
    key = jax.random.key(seed)
    ks = jax.random.split(key, 20)
    D = D_MODEL

    def nrm(k, shape, scale):
        return jax.random.normal(k, shape, F32) * scale

    dt = jnp.exp(jax.random.uniform(ks[16], (N_GDN, 2, GDN_V_HEADS), F32,
                                    math.log(1e-3), math.log(1e-1)))
    return {
        "x": nrm(ks[0], (BATCH, SEQ, D), 1.0),
        "c": nrm(ks[1], (BATCH, D), 1.0),
        "ctx": nrm(ks[2], (BATCH, CTX_LEN, D), 1.0),
        "c_ctx": nrm(ks[3], (D,), 1.0),
        "ada_w": nrm(ks[4], (DEPTH, D, 3 * D), 0.5 * D ** -0.5),
        "ada_b": nrm(ks[5], (DEPTH, 3 * D), 0.02),
        "norm_w": 1.0 + nrm(ks[6], (DEPTH, D), 0.02),
        "mla_w_in": nrm(ks[7], (N_MLA, D, MLA_IN), D ** -0.5),
        "mla_q_norm": 1.0 + nrm(ks[8], (N_MLA, Q_LORA), 0.02),
        "mla_w_uq": nrm(ks[9], (N_MLA, Q_LORA, MLA_HEADS * MLA_QK), Q_LORA ** -0.5),
        "mla_kv_norm": 1.0 + nrm(ks[10], (N_MLA, KV_LORA), 0.02),
        "mla_w_ukv": nrm(ks[11], (N_MLA, KV_LORA, MLA_HEADS * (MLA_NOPE + MLA_V)), KV_LORA ** -0.5),
        "mla_w_o": nrm(ks[12], (N_MLA, MLA_WIDTH, D), MLA_WIDTH ** -0.5),
        "gdn_w_in": nrm(ks[13], (N_GDN, D, GDN_IN), D ** -0.5),
        "gdn_conv_w": nrm(ks[14], (N_GDN, CONV_W, GDN_CONV_CH), CONV_W ** -0.5),
        "gdn_a_log": jnp.log(jax.random.uniform(ks[15], (N_GDN, 2, GDN_V_HEADS), F32, 1.0, 16.0)),
        "gdn_dt_bias": dt + jnp.log(-jnp.expm1(-dt)),
        "gdn_o_norm": 1.0 + nrm(ks[17], (N_GDN, GDN_DV), 0.02),
        "gdn_w_o": nrm(ks[18], (N_GDN, GDN_VAL, D), GDN_VAL ** -0.5),
        "final_norm": 1.0 + nrm(ks[19], (D,), 0.02),
    }

def reference(x, c, ctx, c_ctx, ada_w, ada_b, norm_w, mla_w_in, mla_q_norm, mla_w_uq,
              mla_kv_norm, mla_w_ukv, mla_w_o, gdn_w_in, gdn_conv_w, gdn_a_log,
              gdn_dt_bias, gdn_o_norm, gdn_w_o, final_norm):
    cos, sin = _axial_rope_tables(x.shape[1])
    h_ctx = ctx
    for i in range(DEPTH):
        need_ctx_out = i < DEPTH - 1
        sh, sc, gt = _adaln(c, ada_w[i], ada_b[i])
        shc, scc, gtc = _adaln(c_ctx, ada_w[i], ada_b[i])
        a_in = _rmsnorm(x, norm_w[i]) * (1.0 + sc[:, None]) + sh[:, None]
        c_in = _rmsnorm(h_ctx, norm_w[i]) * (1.0 + scc) + shc
        j = i // N_MIXERS
        if i % N_MIXERS == 0:
            y, y_ctx = _mla_mixer(a_in, c_in, cos, sin, mla_w_in[j], mla_q_norm[j], mla_w_uq[j],
                                  mla_kv_norm[j], mla_w_ukv[j], mla_w_o[j], need_ctx_out)
        else:
            y, y_ctx = _gdn_mixer(a_in, c_in, gdn_w_in[j], gdn_conv_w[j], gdn_a_log[j],
                                  gdn_dt_bias[j], gdn_o_norm[j], gdn_w_o[j], need_ctx_out)
        x = x + gt[:, None] * y.astype(x.dtype)
        if need_ctx_out:
            h_ctx = h_ctx + gtc * y_ctx.astype(h_ctx.dtype)
    return _rmsnorm(x, final_norm)


_drawn_inputs = setup_inputs


def setup_inputs(seed=0):
    import zlib

    import numpy as np

    out = dict(_drawn_inputs(seed))
    spreads = {}
    factors = {'ada_b': 3.428,
     'norm_w': 8.0,
     'mla_q_norm': 8.0,
     'mla_w_uq': 3.535,
     'mla_kv_norm': 8.0,
     'gdn_o_norm': 8.0,
     'final_norm': 2.915}
    for name, (base, spread) in spreads.items():
        noise = np.random.default_rng([zlib.crc32(name.encode()), seed]).standard_normal(out[name].shape)
        drawn = base * np.exp(spread * noise) if base else spread * noise
        out[name] = __import__('jax').numpy.asarray(drawn.astype(out[name].dtype))
    for name, factor in factors.items():
        out[name] = (out[name] * factor).astype(out[name].dtype)
    return out
```

```python
import concourse.bass as bass
import numpy as np
from concourse import mybir
from contextlib import ExitStack

F32 = mybir.dt.float32
F32R = mybir.dt.float32r
ALU = mybir.AluOpType
ACT = mybir.ActivationFunctionType
AXX = mybir.AxisListType.X
ds = bass.ds

P = 128
D = 2048
KC = D // P
SEG = 256
TOK = 2 * SEG
EPS = 1e-6
HEADS = 16
NOPE, ROPE, VD = 128, 64, 128
LORA = 512
LC = LORA // P
QK_SCALE = float((NOPE + ROPE) ** -0.5)
KH, VH = 16, 32
DK = 128
CH = 128
NCH = TOK // CH
ZCOL_MLA = 2 * LORA + ROPE
Q_COL, K_COL, V_COL, Z_COL, BA_COL = 0, 2048, 4096, 8192, 12288
T_IN, T_Z, T_KR, T_HEAD, T_WO, T_BA, T_GDN = 0, 8, 24, 25, 41, 57, 58
T_WO2 = T_GDN + 6 * KH
N_TILES = T_WO2 + 2 * KC
R_NORM, R_QN, R_KVN, R_FIN, R_ON, R_C, R_CC, R_ADA, R_CONV = 0, 32, 36, 40, 56, 57, 73, 89, 185
N_ROWS0, N_ADA, N_CONV = 89, 96, 320
N_COLS = N_ROWS0 + N_ADA + N_CONV
C_IDENT, C_PERM, C_ROPE = 0, 128, 192
C_A = 704
G_INCL, G_STRICT, G_M = 0, 256, 512
LEVELS = 7
C_G = G_M + LEVELS * P
C_ALL = C_A + C_G
CHUNK_ORDER = ((0, 1, 2, 3), (1, 0, 3, 2))


def shape_constants():
    c = np.zeros((P, C_ALL), np.float32)
    i = np.arange(P)
    c[:, C_IDENT:C_IDENT + P] = np.eye(P)
    half = ROPE // 2
    for a in range(half):
        c[a + half, C_PERM + a] = -1.0
        c[a, C_PERM + a + half] = 1.0
    t = np.arange(SEG)
    inv = np.float32(10000.0) ** (-np.arange(0, half, 2, dtype=np.float32) / np.float32(half))
    ang = np.concatenate([(t // 64).astype(np.float32)[:, None] * inv,
                          (t % 64).astype(np.float32)[:, None] * inv], axis=-1).astype(np.float32)
    c[:ROPE, C_ROPE:C_ROPE + SEG] = np.tile(np.cos(ang).T, (2, 1))
    c[:ROPE, C_ROPE + SEG:C_ROPE + 2 * SEG] = np.tile(np.sin(ang).T, (2, 1))
    r, q = i[:, None], i[None, :]
    g = c[:, C_A:]
    g[:, G_INCL:G_INCL + P] = r <= q
    g[:, G_INCL + P:G_INCL + 2 * P] = r >= q
    g[:, G_STRICT:G_STRICT + P] = r < q
    g[:, G_STRICT + P:G_STRICT + 2 * P] = r > q
    for n in range(LEVELS):
        s = 1 << n
        g[:, G_M + n * P:G_M + (n + 1) * P] = (r // (2 * s) == q // (2 * s)) & (r // s != q // s)
    return c


class Linked:

    def __init__(self, eng, sem):
        self.eng, self.sem, self.n = eng, sem, 0

    def restart(self):
        self.eng.sem_clear(self.sem)
        self.n = 0

    def __call__(self, ins):
        self.n += 1
        ins.then_inc(self.sem, 1)
        self.eng.wait_ge(self.sem, self.n)


def build(nc, x, c, ctx_in, c_ctx, ada_w, ada_b, norm_w, mla_w_in, mla_q_norm, mla_w_uq, mla_kv_norm,
          mla_w_ukv, mla_w_o, gdn_w_in, gdn_conv_w, gdn_a_log, gdn_dt_bias, gdn_o_norm, gdn_w_o,
          final_norm, consts, out, gated_dram, gcum_dram, resid_dram):
    with ExitStack() as es:
        base = (nc.sbuf_base + 63) // 64 * 64

        offs = {}

        def at(name, shape, off, dt=F32):
            offs[name] = off
            return nc.alloc_sbuf_tensor_at(name, shape, dt, offset=base + off)

        def sem(name):
            return es.enter_context(nc.semaphore(name))

        KB = 1024
        xT = at("xT", [P, 2, KC, SEG], 0)
        aH = at("aH", [P, KC, TOK], 32 * KB, F32R)
        aL = at("aL", [P, KC, TOK], 64 * KB, F32R)
        zT = at("zT", [P, HEADS, TOK], 96 * KB)
        raw = [at(f"raw{s}", [P, D], (128 + 8 * s) * KB) for s in range(2)]
        wH = [at(f"wH{s}", [P, D], (144 + 8 * s) * KB, F32R) for s in range(2)]
        wL = [at(f"wL{s}", [P, D], (160 + 8 * s) * KB, F32R) for s in range(2)]
        lat = at("lat", [P, 2 * LC, TOK], 176 * KB)
        o = 192 * KB
        K = at("K", [P, C_A], o); o += C_A * 4
        cols = at("cols", [P, 512], o); o += 2048
        mod = at("mod", [P, 6 * KC * 2], o); o += 768
        s1 = at("s1", [P, 2, KC, 2], o); o += 256
        ones = at("ones", [P, P], o); o += 512
        krT = at("krT", [ROPE, TOK], o); o += 2048
        rstd = at("rstd", [P, TOK], o); o += 2048
        cpad = at("cpad", [P, KC, 32], o); o += 2048
        stat = at("stat", [P, 64], o); o += 256
        epsc = at("epsc", [P, 1], o); o += 32
        hb = at("hb", [P, 4], o); o += 32
        oT = at("oT", [P, SEG], o); o += 1024
        nrm = at("nrm", [P, 16], o); o += 64
        sl = at("sl", [P, 5, NCH, 4], o); o += 320
        sd = at("sd", [P, 4, NCH, 4], o); o += 256
        rq = at("rq", [P, 8], o); o += 32
        assert base + o <= 229344, (base + o)
        ident = K[:, C_IDENT:C_IDENT + P]
        perm = K[0:ROPE, C_PERM:C_PERM + ROPE]
        rcos = K[0:ROPE, C_ROPE:C_ROPE + SEG]
        rsin = K[0:ROPE, C_ROPE + SEG:C_ROPE + 2 * SEG]
        rows = at("rows", [P, 5, P], 176 * KB)
        sil = at("sil", [P, 64], 180 * KB)
        tokin = [at(f"tokin{s}", [P, D], (64 + 8 * s) * KB) for s in range(4)]
        adaw = [at(f"adaw{s}", [P, D], (32 + 8 * s) * KB) for s in range(4)]
        adaS = at("adaS", [P, 512], 182 * KB)
        tanh_of = [rstd[:], cpad[:].rearrange("p k m -> p (k m)")]
        sq = [at(f"sq{s}", [P, 2, SEG], (184 + 2 * s) * KB) for s in range(2)]
        xn = [at(f"xn{s}", [P, 2, SEG], (176 + 2 * s) * KB) for s in range(2)]
        an = [at(f"an{s}", [P, TOK], (180 + 2 * s) * KB) for s in range(2)]
        latH = at("latH", [P, 2 * LC, TOK], 32 * KB, F32R)
        latL = at("latL", [P, 2 * LC, TOK], 48 * KB, F32R)
        lsq = at("lsq", [P, 2 * LC, TOK], 64 * KB)
        qT = [at(f"qT{s}", [P, TOK], (64 + 2 * s) * KB) for s in range(2)]
        kT = [at(f"kT{s}", [P, TOK], (68 + 2 * s) * KB) for s in range(2)]
        qrT = [at(f"qrT{s}", [ROPE, TOK], (72 + 2 * s) * KB) for s in range(2)]
        vv = [at(f"vv{s}", [P, NCH, P], (76 + 2 * s) * KB) for s in range(2)]
        pr = [at(f"pr{s}", [P, TOK], (80 + 2 * s) * KB) for s in range(4)]
        pT = at("pT", [P, 6, SEG], 88 * KB)
        rt = at("rt", [ROPE, 2, SEG], 94 * KB)
        lrt = at("lrt", [P, 2, TOK], 88 * KB)
        yT = at("yT", [P, KC, SEG], 96 * KB)
        yout = at("yout", [P, 2, D], 64 * KB)

        G = at("G", [P, C_G], 0)
        z1 = C_G * 4

        def z1t(name, shape, n):
            nonlocal z1
            z1 += n
            return at(name, shape, z1 - n)
        AT = z1t("AT", [P, 2, NCH, P], 4096)
        BT = z1t("BT", [P, 2, NCH, P], 4096)
        XF = z1t("XF", [P, 2, NCH, P], 4096)
        YT = z1t("YT", [P, 2, NCH, P], 4096)
        DT = z1t("DT", [P, 2, NCH, P], 4096)
        pad0 = z1t("pad0", [P, 2, SEG + 4], 2080)
        SS = z1t("SS", [P, 2, P], 1024)
        assert z1 <= 32 * KB, z1
        z1 = 96 * KB
        Gm = z1t("Gm", [P, 2, NCH, P], 4096); Qm = z1t("Qm", [P, 2, 2, P], 2048)
        GB = z1t("GB", [P, 2, TOK], 4096)
        Pc = z1t("Pc", [P, 2, NCH, P], 4096)
        ktok = z1t("ktok", [P, NCH, P], 2048)
        vt = [z1t(f"vt{v}", [P, NCH, P], 2048) for v in range(2)]
        kTc = z1t("kTc", [P, TOK], 2048); qTc = z1t("qTc", [P, SEG], 1024)
        zs = z1t("zs", [P, 2, SEG], 2048)
        qkd = z1t("qkd", [P, 2, 2, P], 2048); kdec = z1t("kdec", [P, 2, 3, P], 3072)
        assert z1 <= 128 * KB, z1
        z1 = 176 * KB
        sc = z1t("sc", [P, 5, NCH, 64], 5120)
        kTn = z1t("kTn", [P, TOK], 2048); qTn = z1t("qTn", [P, SEG], 1024)
        vTn = [z1t(f"vTn{v}", [P, TOK], 2048) for v in range(2)]
        zsn = z1t("zsn", [P, 2, SEG], 2048); cv = z1t("cv", [P, 2, SEG], 2048)
        assert z1 <= 192 * KB, z1
        sqs = at("sqs", [P, 3 * SEG], offs["XF"])
        pad1 = at("pad1", [P, 2, SEG + 4], 192 * KB + 512)
        pad = [pad0, pad1]
        RR = at("RR", [P, 2, P], offs["cpad"]); VN = at("VN", [P, 2, P], offs["cpad"] + 1024)
        oo = at("oo", [P, 2, P], offs["krT"]); og = at("og", [P, 2, P], offs["krT"] + 1024)
        th = rstd
        ba = at("ba", [P, TOK], 96 * KB); bt = at("bt", [P, TOK], 98 * KB); bu = at("bu", [P, TOK], 100 * KB)
        batok = at("batok", [P, NCH, P], 102 * KB); gT = at("gT", [2 * VH, TOK], 104 * KB)
        oraw = at("oraw", [P, VH, SEG], 96 * KB)
        oH = at("oH", [P, VH, SEG], 32 * KB, F32R); oL = at("oL", [P, VH, SEG], 64 * KB, F32R)

        bank = [es.enter_context(nc.psum_tensor(f"bank{b}", [P, 512], F32)) for b in range(8)]

        always = sem("always")
        c_in = sem("constants_in"); r_in = sem("rows_in"); t_in = [sem(f"tokens_in{s}") for s in range(4)]
        rows_T = sem("rows_transposed"); cols_ok = sem("columns_ready")
        ones_ok = sem("ones_ready"); cpad_ok = sem("conditions_ready")
        tokT = sem("tokens_transposed"); tok_act = sem("tokens_copied_act"); tok_dve = sem("tokens_copied_dve")
        a_in = [sem(f"ada_weights_in{s}") for s in range(4)]
        a_used = sem("ada_weights_used"); a_row = sem("ada_rows_copied")
        a_T = sem("ada_rows_transposed"); a_mod = sem("modulation_ready")
        w_in = [sem(f"weights_in{s}") for s in range(2)]
        w_hi = sem("weights_hi"); w_lo = sem("weights_lo"); w_used = sem("weights_used")
        n_sq = sem("squares_ready"); n_sqf = sem("squares_used"); n_sum = sem("square_sums_ready")
        n_rt = sem("norm_roots_ready"); n_ms = sem("mean_squares_ready"); n_a = sem("normed_ready")
        n_hi = sem("normed_hi"); n_lo = sem("normed_lo")
        i_act = sem("in_copied_act"); i_z = sem("gate_ready")
        i_tanh = sem("gate_tanh_ready")
        l_sq = sem("latent_squares"); l_sum = sem("latent_sums"); l_ms = sem("latent_means")
        l_rt = sem("latent_roots"); l_n = sem("latent_normed"); l_hi = sem("latent_hi"); l_lo = sem("latent_lo")
        kr_sw = sem("key_rope_swapped"); kr_ok = sem("key_rope_ready")
        h_qr = sem("head_qr_summed"); h_q = sem("head_q_summed"); h_k = sem("head_k_summed")
        h_sw = sem("head_qr_swapped")
        h_qrc = sem("head_qr_copied"); h_rope = sem("head_qr_rotated")
        h_qkv = sem("head_qkv_copied")
        h_s = sem("scores_ready"); h_mx = sem("score_maxima_ready"); h_e = sem("exponentials_ready")
        h_p = sem("probs_ready"); h_pt = sem("probs_transposed"); h_ptc = sem("prob_transposes_copied_act")
        h_ptd = sem("prob_transposes_copied_dve"); h_o = sem("head_out_summed"); h_g = sem("head_gated")
        g_hi = sem("gated_hi"); g_lo = sem("gated_lo"); o_ev = sem("residual_updated")
        x_out = sem("residual_stored"); x_back = sem("residual_back"); hb_in = sem("head_constants_in")
        g_in = sem("masks_in"); b_th = sem("beta_tanh"); b_e = sem("softplus_exp"); b_l = sem("softplus_log")
        b_a = sem("softplus_arguments"); b_abs = sem("softplus_abs"); b_1 = sem("softplus_plus_one"); b_ea = sem("a_log_exp")
        b_g = sem("betas_and_decays_ready"); b_T = sem("betas_transposed"); b_tok = sem("betas_by_token")
        b_mm = sem("decay_sums"); b_sum = sem("decay_sums_copied"); b_df = sem("decay_differences"); b_ex = sem("decay_exponentials")
        b_gT = sem("decay_sums_transposed"); b_gc = sem("decay_rows_copied"); b_st = sem("decay_rows_stored")
        p_pad = sem("padded"); p_z = sem("z_gate_ready"); c_conv = sem("convolved"); c_tanh = sem("conv_tanh")
        c_silu = sem("conv_silu"); z_tanh = sem("z_tanh"); k_cp = sem("head_inputs_copied"); k_sq = sem("kq_squares")
        u_T = sem("kv_transposed"); u_ss = sem("kq_square_sums"); u_G = sem("gram_ready"); u_Q = sem("kq_products_ready")
        k_tok = sem("k_v0_by_token"); k_tokd = sem("v1_by_token"); k_ms = sem("kq_square_sums_eps"); k_rt = sem("kq_lengths")
        k_G = sem("gram_masked"); k_Q = sem("kq_masked"); k_sc = sem("head_scalars_ready"); k_vr = sem("v_scaled")
        gb_in = sem("decay_rows_in"); d_arg = sem("decay_arguments"); d_exp = sem("decays_ready"); d_AT = sem("systems_ready")
        d_qk = sem("kq_decayed"); b_lv = sem("level_matrices"); x_T = sem("pair_matrices_transposed")
        x_p = sem("level_products"); pc_ = sem("level_products_copied"); x_mm = sem("inverse_changes")
        x_up = sem("inverse_updated"); y_mm = sem("inverse_T_changes"); y_up = sem("inverse_T_updated")
        kd_ = sem("k_decayed"); ch_a = sem("state_read"); ch_b = sem("system_solved"); ch_c = sem("state_products")
        r_ = sem("right_sides"); vn_ = sem("v_new"); s_0 = sem("first_states"); s_up = sem("states_updated")
        e_o = sem("o_summed"); e_ss = sem("o_square_sums"); e_ms = sem("o_mean_squares"); e_rt = sem("o_roots"); e_og = sem("o_gated")
        e_T = sem("o_transposed"); e_cp = sem("o_copied"); e_st = sem("o_stored"); o_back = [sem(f"o_back{q}") for q in range(4)]
        o_hi = sem("o_hi"); o_lo = sem("o_lo")
        f_y = sem("final_normed"); f_T = sem("final_transposed"); f_ev = sem("final_copied")
        stored = sem("output_stored")
        dve_done = sem("vector_step"); act_done = sem("scalar_step")

        wv_in = mla_w_in[0].rearrange("(k p) n -> p k n", p=P)
        wv_uq = mla_w_uq[0].rearrange("(k p) n -> p k n", p=P)
        wv_ukv = mla_w_ukv[0].rearrange("(k p) n -> p k n", p=P)
        wv_o = mla_w_o[0].rearrange("(k p) n -> p k n", p=P)
        wv_o2 = gdn_w_o[0].rearrange("(k p) n -> p k n", p=P)
        wv_g = gdn_w_in[0].rearrange("(k p) n -> p k n", p=P)

        def slot(t0, j):
            return (t0 + j) % 2

        def arrivals(t0, j, i=0):
            return 32 * i + 32 * ((t0 + j) // 2 + 1)

        N_END = 3

        block = es.enter_context(nc.Block())

        @block.sync
        def _(sp):
            sp.sem_inc(always, 1)
            sp.dma_start(K[:], consts[:, 0:C_A]).then_inc(c_in, 16)
            row = lambda v: v.rearrange("a (r p) -> (a r) p", p=P)
            for dst, n, src in ((R_NORM, 32, row(norm_w)), (R_QN, 4, row(mla_q_norm)), (R_KVN, 4, row(mla_kv_norm)),
                                (R_FIN, 16, final_norm.rearrange("(r p) -> r p", p=P)), (R_ON, 1, gdn_o_norm),
                                (R_C, 16, row(c)), (R_CC, 16, c_ctx.rearrange("(r p) -> r p", p=P))):
                sp.dma_start(rows[dst:dst + n, 0, :], src).then_inc(r_in, 16)
            sp.dma_start(rows[0:N_ADA, 1, :], row(ada_b)).then_inc(r_in, 16)
            conv = gdn_conv_w[0].rearrange("k (r p) -> (k r) p", p=P)
            for n, (a, b) in enumerate(((0, 128), (128, 256), (256, 320))):
                sp.dma_start(rows[0:b - a, 2 + n, :], conv[a:b, :]).then_inc(r_in, 16)
            for s in range(4):
                src = (ctx_in if s < 2 else x)[0, (s % 2) * P:(s % 2 + 1) * P, :]
                sp.dma_start(tokin[s][:], src).then_inc(t_in[s], 16)
            for lay in range(2):
                parts = ada_w[lay].rearrange("(k p) n -> k p n", p=P)
                with sp.Fori(0, 3) as i:
                    for k in range(KC):
                        sp.wait_ge(a_used, i * KC + (3 * lay * KC + k + 1))
                        sp.dma_start(adaw[k % 4][:], parts[k, :, ds(i * D, D)]).then_inc(a_in[k % 4], 16)

            def load(t, s, cols_of):
                sp.wait_ge(w_lo, t + 1)
                for dst, src in cols_of(raw[s]):
                    sp.dma_start(dst, src).then_inc(w_in[s], 16)

            def whole(view, col, k0=0):
                def f(r):
                    v = r[:].rearrange("p (k n) -> p k n", k=KC)
                    return [(v[:, a:a + 8, :], view[:, k0 + a:k0 + a + 8, ds(col, P)]) for a in (0, 8)]
                return f

            with sp.Fori(0, 4) as i:
                for j in range(2):
                    load(T_IN + i * 2 + j, slot(T_IN, j), whole(wv_in, i * 2 * P + j * P))
            with sp.Fori(0, 8) as i:
                for j in range(2):
                    load(T_Z + i * 2 + j, slot(T_Z, j), whole(wv_in, i * 2 * P + (ZCOL_MLA + j * P)))

            def kr_cols(r):
                v = r[:, 0:KC * ROPE].rearrange("p (k n) -> p k n", k=KC)
                return [(v[:, a:a + 8, :], wv_in[:, a:a + 8, 2 * LORA:2 * LORA + ROPE]) for a in (0, 8)]
            load(T_KR, slot(T_KR, 0), kr_cols)

            def head_cols(h):
                def f(r):
                    v = r[:, 0:LC * 448].rearrange("p (k n) -> p k n", k=LC)
                    return [(v[:, :, 0:192], wv_uq[:, :, ds(h * 192, 192)]),
                            (v[:, :, 192:448], wv_ukv[:, :, ds(h * 256, 256)])]
                return f
            with sp.Fori(0, HEADS // 2) as i:
                for j in range(2):
                    load(T_HEAD + i * 2 + j, slot(T_HEAD, j), head_cols(i * 2 + j))
            with sp.Fori(0, KC // 2) as i:
                for j in range(2):
                    load(T_WO + i * 2 + j, slot(T_WO, j), whole(wv_o, i * 2 * P + j * P))
            load(T_BA, slot(T_BA, 0), whole(wv_g, BA_COL))

            def head_tile(h, n):
                col = (h * P + Q_COL, h * P + K_COL, h * 256 + V_COL, h * 256 + (V_COL + P),
                       h * 256 + Z_COL, h * 256 + (Z_COL + P))[n]
                load(h * 6 + (T_GDN + n), slot(T_GDN, n), whole(wv_g, col))

            def decay_rows(h, v):
                sp.wait_ge(d_arg, h * 2 + (v + 1))
                for d in range(2):
                    sp.dma_start(GB[:, d, :], gcum_dram[ds(h * 2 + (d * VH + v), 1), :].rearrange("o t -> (o t)").partition_broadcast(P)
                                 ).then_inc(gb_in, 16)

            for n in range(6):
                head_tile(0, n)
            sp.wait_ge(b_st, 16)
            decay_rows(0, 0)
            with sp.Fori(0, KH - 1) as h:
                for v in range(2):
                    for n in range(3 * v, 3 * v + 2):
                        head_tile(h + 1, n)
                    decay_rows(h + v, 1 - v)
                    head_tile(h + 1, 3 * v + 2)
            for half in range(2):
                load(T_WO2 + half, half, whole(wv_o2, 0, half * KC))
            decay_rows(KH - 1, 1)
            sp.wait_ge(e_st, 16 * VH + 16)
            sp.wait_ge(e_cp, VH)
            sp.dma_start(xT[:, 1, :, :].rearrange("p k t -> p (k t)"), resid_dram[:, :]).then_inc(x_back, 16)
            for q in range(4):
                sp.dma_start(oraw[:, 8 * q:8 * q + 8, :], gated_dram[8 * q:8 * q + 8].rearrange("h p t -> p h t")).then_inc(o_back[q], 16)
            with sp.Fori(1, KC) as i:
                for half in range(2):
                    load(i * 2 + (T_WO2 + half), half, whole(wv_o2, i * P, half * KC))
            for g in range(4):
                sp.wait_ge(f_ev, 2 * g + 2)
                for tt in range(2):
                    sp.dma_start(out[0, tt * P:(tt + 1) * P, g * 512:(g + 1) * 512],
                                 yout[:, tt, g * 512:(g + 1) * 512]).then_inc(stored, 16)
            sp.wait_ge(stored, 8 * 16)

        @block.tensor
        def _(pe):
            mm = nc.tensor.matmul

            def transpose(out_, in_, n):
                return nc.tensor.transpose(out_, in_, ident[0:n, 0:n])

            pe.wait_ge(c_in, 16)
            pe.wait_ge(r_in, 12 * 16 - 16)
            at_col = 0
            for n, cnt in enumerate((N_ROWS0, N_ADA, 128, 128, 64)):
                last = transpose(bank[4][:, at_col:at_col + cnt], rows[0:cnt, n, :], cnt)
                at_col += cnt
            last.then_inc(rows_T, 1)
            for g in range(16):
                s, q = g // 4, g % 4
                if q == 0:
                    pe.wait_ge(t_in[s], 16)
                if g >= 4:
                    pe.wait_ge((tok_act, tok_dve)[g % 2], (g - 4) // 2 + 1)
                for m in range(4):
                    last = transpose(bank[g % 4][:, m * P:(m + 1) * P], tokin[s][:, (4 * q + m) * P:(4 * q + m + 1) * P], P)
                last.then_inc(tokT, 1)
            pe.sem_inc(a_used, 4)
            pe.sem_inc(a_T, 1)
            pe.wait_ge(cpad_ok, 1)
            with pe.Fori(0, 6) as i:
                pe.wait_ge(a_row, i + 1)
                for k in range(KC):
                    pe.wait_ge(a_in[k % 4], i * 64 + (k // 4 + 1) * 16)
                    for j in range(4):
                        last = mm(bank[7][32 * j:32 * j + 32, :], cpad[:, k, :], adaw[k % 4][:, j * 512:(j + 1) * 512],
                                  start=(k == 0), stop=(k == KC - 1))
                    last.then_inc(a_used, 1)
                pe.wait_ge(a_row, i + 2)
                pe.wait_ge(a_mod, i + 1)
                for b in range(4):
                    last = transpose(bank[6][:, b * P:(b + 1) * P], adaS[:, b * P:(b + 1) * P], P)
                last.then_inc(a_T, 1)

            def sums(n, cnt=TOK):
                for k in range(KC):
                    pe.wait_ge(n_sq, n * KC + k + 1)
                    last = mm(bank[0][:, 0:cnt], ones[:], sq[k % 2][:].rearrange("p s t -> p (s t)")[:, 0:cnt],
                              start=(k == 0), stop=(k == KC - 1))
                    last.then_inc(n_sqf, 1)
            sums(0)

            def product(dst, w, col, width, n, kcs, hi, lo, tok=slice(0, TOK)):
                steps = len(kcs) * 3
                s = 0
                wh = wH[w][:, 0:n[0] * n[1]].rearrange("p (k n) -> p k n", k=n[0])
                wl = wL[w][:, 0:n[0] * n[1]].rearrange("p (k n) -> p k n", k=n[0])
                for k, ka in kcs:
                    for wt, act in ((wh, hi), (wh, lo), (wl, hi)):
                        last = mm(dst, wt[:, k, col:col + width], act[:, ka, tok], start=(s == 0), stop=(s == steps - 1))
                        s += 1
                return last

            full = [(k, k) for k in range(KC)]
            pe.sem_inc(w_used, 2)
            pe.wait_ge(n_lo, KC)
            with pe.Fori(0, 4) as i:
                for j in range(2):
                    pe.wait_ge(w_lo, i * 2 + (T_IN + j + 3))
                    pe.wait_ge(i_act, i * 2 + (j + 1))
                    product(bank[j][:], slot(T_IN, j), 0, P, (KC, P), full, aH, aL).then_inc(w_used, 1)
            pe.wait_ge(i_act, T_Z + 2)
            with pe.Fori(0, 8) as i:
                for j in range(2):
                    pe.wait_ge(w_lo, i * 2 + (T_Z + j + 3))
                    pe.wait_ge(i_z, i * 2 + (j + 1))
                    product(bank[j][:], slot(T_Z, j), 0, P, (KC, P), full, aH, aL).then_inc(w_used, 1)
            pe.wait_ge(w_lo, T_KR + 3)
            pe.wait_ge(i_z, 17)
            product(bank[0][0:ROPE, :], slot(T_KR, 0), 0, ROPE, (KC, ROPE), full, aH, aL).then_inc(w_used, 1)
            for which in range(2):
                pe.wait_ge(l_sq, which + 1)
                for k in range(LC):
                    last = mm(bank[2 + which][:], ones[:], lsq[:, which * LC + k, :], start=(k == 0), stop=(k == LC - 1))
                last.then_inc(l_sum, 1)
            pe.wait_ge(i_z, 18)
            pe.wait_ge(i_act, 11)
            mm(bank[1][0:ROPE, 0:SEG], perm, krT[:, SEG:TOK], start=True, stop=True).then_inc(kr_sw, 1)

            def project(h, s):
                w = slot(T_HEAD, s)
                pe.wait_ge(w_lo, h + (T_HEAD + 3))
                pe.wait_ge(h_rope, h + 1)
                n = (LC, 448)
                own = [(k, k) for k in range(LC)]
                kv = [(k, LC + k) for k in range(LC)]
                product(bank[2][0:ROPE, :], w, NOPE, ROPE, n, own, latH, latL).then_inc(h_qr, 1)
                pe.wait_ge(h_qkv, h * 3 + 3)
                product(bank[0][:], w, 0, NOPE, n, own, latH, latL).then_inc(h_q, 1)
                product(bank[1][:], w, 192, NOPE, n, kv, latH, latL).then_inc(h_k, 1)
                wh = wH[w][:, 0:LC * 448].rearrange("p (k n) -> p k n", k=LC)
                wl = wL[w][:, 0:LC * 448].rearrange("p (k n) -> p k n", k=LC)
                for tt in range(NCH):
                    step = 0
                    for k in range(LC):
                        for act, wt in ((latH, wh), (latH, wl), (latL, wh)):
                            last = mm(bank[3][:, tt * P:(tt + 1) * P], act[:, LC + k, tt * P:(tt + 1) * P],
                                      wt[:, k, 320:448], start=(step == 0), stop=(step == 11))
                            step += 1
                last.then_inc(w_used, 1)
                pe.wait_ge(always, 1)
                pe.wait_ge(h_qrc, h + 1)
                mm(bank[2][0:ROPE, 0:SEG], perm, qrT[s][:, SEG:TOK], start=True, stop=True).then_inc(h_sw, 1)

            def scores(h, s):
                pe.wait_ge(h_qkv, h * 3 + 6)
                pe.wait_ge(h_rope, h + 2)
                pe.wait_ge(h_ptc, h * 2 + 2)
                pe.wait_ge(h_ptd, h + 1)
                pe.wait_ge(h_g, h + 1)
                for qt in range(4):
                    n = SEG if qt < 2 else TOK
                    mm(bank[4 + qt][:, 0:n], qT[s][:, qt * P:(qt + 1) * P], kT[s][:, 0:n], start=True, stop=False)
                    mm(bank[4 + qt][:, 0:n], qrT[s][:, qt * P:(qt + 1) * P], krT[:, 0:n],
                       start=False, stop=True).then_inc(h_s, 1)

            def attend(h, s):
                pe.wait_ge(h_p, h * 4 + 4)
                for b, (kts, q0) in enumerate((((0, 1), 2), ((2, 3), 2), ((0, 1), 0))):
                    for m, kt in enumerate(kts):
                        for qq in range(2):
                            last = transpose(bank[4 + b][:, m * SEG + qq * P:m * SEG + (qq + 1) * P],
                                             pr[q0 + qq][:, kt * P:(kt + 1) * P], P)
                    last.then_inc(h_pt, 1)
                pe.wait_ge(h_ptd, h + 2)
                pe.wait_ge(h_ptc, h * 2 + 4)
                for n, kt in enumerate((0, 1)):
                    mm(bank[7][:, 0:SEG], vv[s][:, kt, :], pT[:, 4 + n, :], start=(n == 0), stop=(n == 1))
                for kt in range(4):
                    last = mm(bank[7][:, SEG:TOK], vv[s][:, kt, :], pT[:, kt, :], start=(kt == 0), stop=(kt == 3))
                last.then_inc(h_o, 1)

            pe.wait_ge(l_lo, 2)
            pe.wait_ge(kr_ok, 1)
            project(0, 0)
            with pe.Fori(0, HEADS // 2 - 1) as i:
                for j in range(2):
                    scores(i * 2 + j, j)
                    project(i * 2 + (j + 1), 1 - j)
                    attend(i * 2 + j, j)
            scores(HEADS - 2, 0)
            project(HEADS - 1, 1)
            attend(HEADS - 2, 0)
            scores(HEADS - 1, 1)
            attend(HEADS - 1, 1)

            pe.wait_ge(g_lo, 4)
            with pe.Fori(0, KC // 2) as i:
                for j in range(2):
                    pe.wait_ge(w_lo, i * 2 + (T_WO + j + 3))
                    pe.wait_ge(o_ev, i * 2 + (j + 1))
                    product(bank[j][:], slot(T_WO, j), 0, P, (KC, P), full, aH, aL).then_inc(w_used, 1)

            sums(1)
            pe.wait_ge(w_lo, T_BA + 3)
            pe.wait_ge(n_lo, 2 * KC)
            product(bank[1][:], slot(T_BA, 0), 0, P, (KC, P), full, aH, aL).then_inc(w_used, 1)
            pe.wait_ge(b_g, 2)
            for cc in range(NCH):
                last = transpose(bank[2][:, cc * P:(cc + 1) * P], ba[:, cc * P:(cc + 1) * P], P)
            last.then_inc(b_T, 1)
            pe.wait_ge(b_tok, 1)
            pe.wait_ge(g_in, 16)
            for cc in range(NCH):
                for d in range(2):
                    mm(bank[3][:, cc * 64 + d * 32:cc * 64 + d * 32 + 32], G[:, G_INCL + d * P:G_INCL + (d + 1) * P],
                       batok[:, cc, 64 + 32 * d:96 + 32 * d], start=True, stop=True)
                last = mm(bank[3][:, 256 + cc * 64:256 + cc * 64 + 64], ones[:], batok[:, cc, 64:128], start=True, stop=True)
            last.then_inc(b_mm, 1)
            pe.wait_ge(b_sum, 1)
            for cc in range(NCH):
                last = transpose(bank[4][0:64, cc * P:(cc + 1) * P], sc[:, 0, cc, :], P)
            last.then_inc(b_gT, 1)

            def piece(h, n):
                tile, part = n // 8, n % 8
                if part == 0:
                    pe.wait_ge(w_lo, h * 6 + (T_GDN + tile + 3))
                    if tile < 2:
                        pe.wait_ge(p_z, h * 2 + (tile + 1))
                    else:
                        pe.wait_ge(p_pad, h * 4 + (tile - 1))
                w, dst = slot(T_GDN, tile), bank[tile % 2]
                wh = wH[w][:].rearrange("p (k n) -> p k n", k=KC)
                wl = wL[w][:].rearrange("p (k n) -> p k n", k=KC)
                for k in (2 * part, 2 * part + 1):
                    lo = 0 if tile in (1, 2, 3) else SEG
                    for m, (wt, a) in enumerate(((wh, aH), (wh, aL), (wl, aH))):
                        last = mm(dst[:, 0:TOK - lo], wt[:, k, :], a[:, k, lo:TOK], start=(k == 0 and m == 0),
                                  stop=(k == KC - 1 and m == 2))
                if part == 7:
                    last.then_inc(w_used, 1)

            def turn_out(h, v):
                pe.wait_ge(e_og, h * 2 + (v + 1))
                for tt in range(2):
                    last = transpose(bank[7][:, tt * P:(tt + 1) * P], og[:, tt, :], P)
                last.then_inc(e_T, 1)

            def core(h, more):
                pe.wait_ge(c_silu, h * 4 + 4 + 1)
                for n, src in enumerate((kTn, vTn[0], vTn[1])):
                    for cc in range(NCH):
                        last = transpose(bank[2 + n][:, cc * P:(cc + 1) * P], src[:, cc * P:(cc + 1) * P], P)
                    last.then_inc(u_T, 1)
                for cc in range(NCH):
                    last = mm(bank[6][:, cc * P:(cc + 1) * P], kTn[:, cc * P:(cc + 1) * P], kTn[:, cc * P:(cc + 1) * P],
                              start=True, stop=True)
                last.then_inc(u_G, 1)
                more(1)
                pe.wait_ge(k_sq, h + 1)
                for xx in range(2):
                    last = mm(bank[7][:, xx * P:(xx + 1) * P], kTn[:, SEG + xx * P:SEG + (xx + 1) * P],
                              qTn[:, xx * P:(xx + 1) * P], start=True, stop=True)
                last.then_inc(u_Q, 1)
                for cc in range(6):
                    last = mm(bank[5][:, cc:cc + 1], sqs[:, cc * P:(cc + 1) * P], ones[:, 0:1], start=True, stop=True)
                last.then_inc(u_ss, 1)
                more(1)
                for v in range(2):
                    more(2)
                    if v:
                        pe.wait_ge(e_o, h * 2 + 2)
                    for d in range(2):
                        pe.wait_ge(b_lv, h * 28 + (v * 14 + d + 1))
                        for cc in range(NCH):
                            last = transpose(bank[4 + d][:, cc * P:(cc + 1) * P], BT[:, d, cc, :], P)
                        last.then_inc(x_T, 1)
                    more(1)
                    for lev in range(1, LEVELS):
                        for d in range(2):
                            pe.wait_ge(b_lv, h * 28 + (v * 14 + lev * 2 + d + 1))
                            pe.wait_ge(x_up, h * 24 + (v * 12 + (lev - 1) * 2 + d + 1))
                            pe.wait_ge(y_up, h * 28 + (v * 14 + (lev - 1) * 2 + d + 1))
                            for cc in range(NCH):
                                last = mm(bank[2 + d][:, cc * P:(cc + 1) * P], BT[:, d, cc, :], XF[:, d, cc, :], start=True, stop=True)
                            last.then_inc(x_p, 1)
                        more(1 if v else 2)
                        for d in range(2):
                            pe.wait_ge(pc_, h * 24 + (v * 12 + (lev - 1) * 2 + d + 1))
                            if lev < LEVELS - 1:
                                for cc in range(NCH):
                                    last = mm(bank[4 + d][:, cc * P:(cc + 1) * P], YT[:, d, cc, :], Pc[:, d, cc, :], start=True, stop=True)
                                last.then_inc(x_mm, 1)
                            for cc in range(NCH):
                                last = mm(bank[2 + d][:, cc * P:(cc + 1) * P], Pc[:, d, cc, :], YT[:, d, cc, :], start=True, stop=True)
                            last.then_inc(y_mm, 1)
                        more(1)
                        if v and lev == 1:
                            turn_out(h, 0)
                    for m in range(NCH):
                        if m:
                            for d in range(2):
                                cc = CHUNK_ORDER[d][m]
                                if m == 1:
                                    pe.wait_ge(s_0, h * 4 + (v * 2 + d + 1))
                                else:
                                    pe.wait_ge(s_up, h * 8 + (v * 4 + (m - 2) * 2 + d + 1))
                                last = mm(bank[4 + d][:, 0:P], kTc[:, cc * P:(cc + 1) * P], SS[:, d, :], start=True, stop=True)
                                if m >= 2:
                                    last = mm(bank[2 + d][:, 0:P], qTc[:, (cc - 2) * P:(cc - 1) * P], SS[:, d, :], start=True, stop=True)
                                last.then_inc(ch_a, 1)
                            more(1)
                        for d in range(2):
                            cc = CHUNK_ORDER[d][m]
                            if m:
                                pe.wait_ge(r_, h * 12 + (v * 6 + (m - 1) * 2 + d + 1))
                            else:
                                pe.wait_ge(y_up, h * 28 + (v * 14 + 12 + d + 1))
                                pe.wait_ge(k_vr, h * 2 + (v + 1))
                            rhs = RR[:, d, :] if m else vt[v][:, cc, :]
                            mm(bank[4 + d][:, P:2 * P], YT[:, d, cc, :], rhs, start=True, stop=True).then_inc(ch_b, 1)
                        if m and not v:
                            more(1)
                        for d in range(2):
                            cc = CHUNK_ORDER[d][m]
                            pe.wait_ge(vn_, h * 16 + (v * 8 + m * 2 + d + 1))
                            if m < 3:
                                if m == 0:
                                    pe.wait_ge(kd_, h * 2 + (v + 1))
                                last = mm(bank[4 + d][:, 2 * P:3 * P], kdec[:, d, m, :], VN[:, d, :], start=True, stop=True)
                            if m >= 2:
                                if m == 2:
                                    pe.wait_ge(d_qk, h * 2 + (v + 1))
                                    pe.wait_ge(e_o, h * 2 + (v + 1))
                                last = mm(bank[6][:, (cc - 2) * P:(cc - 1) * P], qkd[:, d, cc - 2, :], VN[:, d, :],
                                          start=(m == 2 and d == 0), stop=(m == 3), skip_group_check=True)
                            last.then_inc(ch_c, 1)
                    if v:
                        more(3)
                        turn_out(h, v)

            def pieces_of(h):
                at_piece = [0]

                def more(k):
                    for n in range(at_piece[0], min(at_piece[0] + k, 48)):
                        piece(h, n)
                    at_piece[0] = min(at_piece[0] + k, 48)
                return more

            pieces_of(0)(48)
            with pe.Fori(0, KH - 1) as h:
                more = pieces_of(h + 1)
                core(h, more)
                more(48)
            core(KH - 1, lambda k: None)

            with pe.Fori(0, KC // 2) as i:
                for j in range(2):
                    pe.wait_ge(o_ev, i * 2 + (KC + j + 1))
                    pe.wait_ge(o_lo, 4)
                    for half in range(2):
                        pe.wait_ge(w_lo, i * 4 + (T_WO2 + 2 * j + half + 3))
                        wh = wH[half][:].rearrange("p (k n) -> p k n", k=KC)
                        wl = wL[half][:].rearrange("p (k n) -> p k n", k=KC)
                        for k in range(KC):
                            for m, (wt, a) in enumerate(((wh, oH), (wh, oL), (wl, oH))):
                                last = mm(bank[j][:, 0:SEG], wt[:, k, :], a[:, half * KC + k, :],
                                          start=(half == 0 and k == 0 and m == 0), stop=(half == 1 and k == KC - 1 and m == 2))
                        last.then_inc(w_used, 1)

            sums(2, SEG)
            for g in range(4):
                pe.wait_ge(f_y, 4 * g + 4)
                for tt in range(2):
                    b = 4 + (2 * g + tt) % 4
                    if g >= 2:
                        pe.wait_ge(f_ev, 2 * g + tt - 3)
                    for m in range(4):
                        last = transpose(bank[b][:, m * P:(m + 1) * P], yT[:, 4 * g + m, tt * P:(tt + 1) * P], P)
                    last.then_inc(f_T, 1)

        @block.scalar
        def _(act):
            A = nc.scalar.activation
            link = Linked(act, act_done)

            def apart():
                act.wait_ge(always, 1)

            act.wait_ge(rows_T, 1)
            A(cols[:, 0:N_COLS], bank[4][:, 0:N_COLS], ACT.Copy).then_inc(cols_ok, 1)
            act.wait_ge(cols_ok, 1)
            A(sil[:, 0:32], cols[:, R_C:R_C + 32], ACT.Tanh, scale=0.5).then_inc(act_done, 1)
            link.n = 1
            for g in range(0, 16, 2):
                s, q = g // 4, g % 4
                act.wait_ge(tokT, g + 1)
                A(xT[:, s // 2, 4 * q:4 * q + 4, (s % 2) * P:(s % 2 + 1) * P],
                  bank[g % 4][:].rearrange("p (m t) -> p m t", m=4), ACT.Copy).then_inc(tok_act, 1)
            act.sem_inc(a_row, 1)
            with act.Fori(0, 6) as i:
                act.wait_ge(a_used, i * KC + (KC + 4))
                act.wait_ge(a_T, i + 1)
                A(adaS[:], bank[7][:], ACT.Copy).then_inc(a_row, 1)

            def split(t, t0, j, i=0):
                s = slot(t0, j)
                act.wait_ge(w_in[s], arrivals(t0, j, i))
                act.wait_ge(w_used, t + 1)
                A(wH[s][:], raw[s][:], ACT.Copy).then_inc(w_hi, 1)

            def squares(n, segs=2):
                for k in range(KC):
                    if n or k >= 2:
                        act.wait_ge(n_sqf, n * KC + k - 1)
                    A(sq[k % 2][:, 0:segs, :], xT[:, 2 - segs:2, k, :], ACT.Square).then_inc(n_sq, 1)

            def root(n, cnt=TOK):
                act.wait_ge(n_ms, n + 1)
                A(rstd[:, 0:cnt], rstd[:, 0:cnt], ACT.Sqrt).then_inc(n_rt, 1)

            def rounded(n):
                with act.Fori(0, KC // 2) as i:
                    for j in range(2):
                        apart()
                        act.wait_ge(n_a, i * 2 + (n * KC + j + 1))
                        A(aH[:, ds(i * 2 + j, 1), :].rearrange("p o t -> p (o t)"), an[j][:], ACT.Copy).then_inc(n_hi, 1)

            act.wait_ge(tok_dve, 8)
            act.wait_ge(tok_act, 8)
            squares(0)
            root(0)
            split(T_IN, T_IN, 0)
            rounded(0)
            act.sem_inc(i_act, 2)
            with act.Fori(0, 4) as i:
                for j in range(2):
                    split(i * 2 + (T_IN + j + 1), T_IN, j + 1, i)
                    apart()
                    act.wait_ge(w_used, i * 2 + (T_IN + j + 3))
                    A(lat[:, ds(i * 2 + j, 1), :].rearrange("p o t -> p (o t)"), bank[j][:], ACT.Copy).then_inc(i_act, 1)
            with act.Fori(0, 8) as i:
                for j in range(2):
                    split(i * 2 + (T_Z + j + 1), T_Z, j + 1, i)
                    act.wait_ge(w_used, i * 2 + (T_Z + j + 3))
                    act.wait_ge(i_z, i * 2 + (j + 1))
                    A(tanh_of[j], bank[j][:], ACT.Tanh, scale=0.5).then_inc(i_tanh, 1)
            act.wait_ge(w_used, T_KR + 3)
            A(krT[:], bank[0][0:ROPE, :], ACT.Copy).then_inc(i_act, 1)
            act.wait_ge(i_act, 10)
            for which in range(2):
                A(lsq[:, which * LC:(which + 1) * LC, :], lat[:, which * LC:(which + 1) * LC, :], ACT.Square).then_inc(l_sq, 1)
            split(T_HEAD, T_HEAD, 0)
            act.wait_ge(l_ms, 2)
            A(lrt[:], lrt[:], ACT.Sqrt).then_inc(l_rt, 1)
            for which in range(2):
                act.wait_ge(l_n, LC * (which + 1))
                A(latH[:, which * LC:(which + 1) * LC, :], lat[:, which * LC:(which + 1) * LC, :], ACT.Copy).then_inc(l_hi, 1)
            split(T_HEAD + 1, T_HEAD, 1)

            def copy_qkv(h, s):
                act.wait_ge(h_q, h + 1)
                A(qT[s][:], bank[0][:], ACT.Copy).then_inc(h_qkv, 1)
                act.wait_ge(h_k, h + 1)
                A(kT[s][:], bank[1][:], ACT.Copy).then_inc(h_qkv, 1)
                act.wait_ge(w_used, h + (T_HEAD + 3))
                A(vv[s][:].rearrange("p a b -> p (a b)"), bank[3][:], ACT.Copy).then_inc(h_qkv, 1)

            def exponentials(h, s):
                for qt in range(4):
                    n = SEG if qt < 2 else TOK
                    act.wait_ge(h_mx, h * 4 + (qt + 1))
                    A(pr[qt][:, 0:n], bank[4 + qt][:, 0:n], ACT.Exp, bias=stat[:, 16 * s + 4 + qt:16 * s + 5 + qt],
                      scale=QK_SCALE, accum_out=stat[:, 16 * s + 8 + qt:16 * s + 9 + qt]).then_inc(h_e, 1)

            def copy_pT(h):
                act.wait_ge(h_pt, h * 3 + 1)
                A(pT[:, 0:2, :].rearrange("p a b -> p (a b)"), bank[4][:], ACT.Copy).then_inc(h_ptc, 1)
                act.wait_ge(h_pt, h * 3 + 3)
                A(pT[:, 4:6, :].rearrange("p a b -> p (a b)"), bank[6][:], ACT.Copy).then_inc(h_ptc, 1)

            act.sem_inc(h_qkv, 3)
            act.sem_inc(h_ptc, 2)
            copy_qkv(0, 0)
            with act.Fori(0, HEADS // 2 - 1) as i:
                for j in range(2):
                    exponentials(i * 2 + j, j)
                    split(i * 2 + (T_HEAD + j + 2), T_HEAD, j + 2, i)
                    copy_qkv(i * 2 + (j + 1), 1 - j)
                    copy_pT(i * 2 + j)
            exponentials(HEADS - 2, 0)
            split(T_WO, T_WO, 0)
            copy_qkv(HEADS - 1, 1)
            copy_pT(HEADS - 2)
            exponentials(HEADS - 1, 1)
            copy_pT(HEADS - 1)
            act.wait_ge(h_g, HEADS + 1)
            for q in range(4):
                A(aH[:, 4 * q:4 * q + 4, :], zT[:, 4 * q:4 * q + 4, :], ACT.Copy).then_inc(g_hi, 1)
            split(T_WO + 1, T_WO, 1)
            with act.Fori(0, KC // 2) as i:
                for j in range(2):
                    split(i * 2 + (T_WO + j + 2), T_WO, j + 2, i)
            act.wait_ge(o_ev, KC + 2)
            squares(1)
            root(1)
            rounded(1)
            act.wait_ge(n_a, 2 * KC)
            act.dma_start(resid_dram[:, :], xT[:, 1, :, :].rearrange("p k t -> p (k t)")).then_inc(x_out, 16)
            act.dma_start(hb[64:128, 0:1], gdn_dt_bias.rearrange("a d h -> (d h) a")).then_inc(hb_in, 16)
            act.dma_start(hb[64:128, 1:2], gdn_a_log.rearrange("a d h -> (d h) a")).then_inc(hb_in, 16)
            act.wait_ge(x_out, 16)
            act.dma_start(G[:], consts[:, C_A:C_ALL]).then_inc(g_in, 16)
            act.wait_ge(hb_in, 32)
            A(hb[64:128, 2:3], hb[64:128, 1:2], ACT.Exp).then_inc(b_ea, 1)
            act.wait_ge(w_used, T_BA + 3)
            A(bt[0:64, :], bank[1][0:64, :], ACT.Tanh, scale=0.5).then_inc(b_th, 1)
            act.wait_ge(b_a, 1)
            A(bu[64:128, :], bt[64:128, :], ACT.Abs).then_inc(b_abs, 1)
            act.wait_ge(b_abs, 1)
            A(bu[64:128, :], bu[64:128, :], ACT.Exp, scale=-1.0).then_inc(b_e, 1)
            act.wait_ge(b_1, 1)
            A(bu[64:128, :], bu[64:128, :], ACT.Ln).then_inc(b_l, 1)
            split(T_GDN + 1, T_GDN, 1)
            act.wait_ge(b_T, 1)
            A(batok[:].rearrange("p c n -> p (c n)"), bank[2][:], ACT.Copy).then_inc(b_tok, 1)
            act.wait_ge(b_mm, 1)
            A(sc[:, 0, :, :].rearrange("p c n -> p (c n)"), bank[3][:, 0:SEG], ACT.Copy).then_inc(b_sum, 1)
            act.wait_ge(b_sum, 1)
            A(sc[:, 1, :, :], batok[:, :, 0:64], ACT.Copy)
            A(sc[:, 2, :, :].rearrange("p c n -> p (c n)"), sc[:, 0, :, :].rearrange("p c n -> p (c n)"), ACT.Exp)
            A(sc[:, 4, :, :].rearrange("p c n -> p (c n)"), bank[3][:, SEG:TOK], ACT.Exp).then_inc(b_ex, 1)
            act.wait_ge(b_df, 1)
            A(sc[:, 3, :, :].rearrange("p c n -> p (c n)"), sc[:, 3, :, :].rearrange("p c n -> p (c n)"), ACT.Exp).then_inc(b_ex, 1)
            act.wait_ge(b_gT, 1)
            A(gT[:], bank[4][0:64, :], ACT.Copy).then_inc(b_gc, 1)
            act.wait_ge(b_gc, 1)
            act.dma_start(gcum_dram[:, :], gT[:]).then_inc(b_st, 16)

            def tile_act(h, n, stream=True):
                act.wait_ge(w_used, h * 6 + (T_GDN + n + 3))
                if n < 4:
                    act.wait_ge(c_conv, h * 4 + (n + 1))
                    if n == 0:
                        A(pad[0][:, 1, 2:2 + SEG], bank[0][:, 0:SEG], ACT.Copy).then_inc(p_pad, 1)
                    else:
                        A(pad[n % 2][:, :, 2:2 + SEG], bank[n % 2][:].rearrange("p (s t) -> p s t", s=2), ACT.Copy).then_inc(p_pad, 1)
                else:
                    act.wait_ge(c_silu, h * 4 + 5) if n == 4 else act.wait_ge(p_z, h * 2 + 3)
                    A(th[:, 0:SEG], bank[n % 2][:, 0:SEG], ACT.Tanh, scale=0.5).then_inc(z_tanh, 1)
                split(h * 6 + (T_GDN + n + 2), T_GDN, n + 2, h * 3)
                if n < 4:
                    act.wait_ge(c_conv, h * 4 + (n + 3))
                    act.wait_ge(c_silu, h * 4 + (n + 1))
                    src = cv[:, 1:2, :] if n == 0 else cv[:]
                    dst = th[:, SEG:TOK] if n == 0 else th[:]
                    A(dst, src.rearrange("p s t -> p (s t)"), ACT.Tanh).then_inc(c_tanh, 1)

            def store_out(h, v):
                act.wait_ge(e_cp, h * 2 + (v + 1))
                act.dma_start(gated_dram[ds(h * 2 + v, 1)].rearrange("o p t -> p (o t)"), oT[:]).then_inc(e_st, 16)

            def decays_act(n):
                act.wait_ge(d_arg, n + 2)
                A(DT[:].rearrange("p d c n -> p (d c n)"), DT[:].rearrange("p d c n -> p (d c n)"), ACT.Exp).then_inc(d_exp, 1)

            def core_act(h, tile, end=False):
                act.wait_ge(c_silu, h * 4 + 5)
                act.wait_ge(p_z, h * 2 + 4)
                A(sqs[:, 0:TOK], kTn[:], ACT.Square)
                A(sqs[:, TOK:TOK + SEG], qTn[:], ACT.Square).then_inc(k_sq, 1)
                act.wait_ge(u_T, h * 3 + 1)
                A(ktok[:].rearrange("p c n -> p (c n)"), bank[2][:], ACT.Copy).then_inc(k_tok, 1)
                act.wait_ge(u_T, h * 3 + 2)
                A(vt[0][:].rearrange("p c n -> p (c n)"), bank[3][:], ACT.Copy).then_inc(k_tok, 1)
                A(kTc[:], kTn[:], ACT.Copy)
                A(qTc[:], qTn[:], ACT.Copy)
                A(zs[:], zsn[:], ACT.Copy).then_inc(k_cp, 1)
                act.wait_ge(k_ms, h + 1)
                A(nrm[:, 0:6], nrm[:, 0:6], ACT.Sqrt).then_inc(k_rt, 1)
                for v in range(2):
                    act.wait_ge(k_rt, h + 1)
                    act.wait_ge(k_tok, h * 2 + 2)
                    act.wait_ge(k_tokd, h + 1)
                    for cc in range(NCH):
                        last = A(vt[v][:, cc, :], vt[v][:, cc, :], ACT.Copy, scale=nrm[:, cc:cc + 1])
                    last.then_inc(k_vr, 1)
                for v in range(2):
                    for lev in range(1, LEVELS):
                        for d in range(2):
                            act.wait_ge(x_p, h * 24 + (v * 12 + (lev - 1) * 2 + d + 1))
                            A(Pc[:, d].rearrange("p c n -> p (c n)"), bank[2 + d][:], ACT.Copy).then_inc(pc_, 1)
                        if v and lev == 1:
                            store_out(h, 0)
                        if lev in (2, 4):
                            tile(3 * v + lev // 2 - 1)
                    if not (end and v):
                        decays_act(h * 2 + (v + 1))
                    for m in range(NCH):
                        for d in range(2):
                            cc = CHUNK_ORDER[d][m]
                            act.wait_ge(ch_b, h * 16 + (v * 8 + m * 2 + d + 1))
                            A(VN[:, d, :], bank[4 + d][:, P:2 * P], ACT.Copy, scale=sd[:, 1, cc, d * 2 + v:d * 2 + v + 1]).then_inc(vn_, 1)
                        if m == 0:
                            for d in range(2):
                                act.wait_ge(ch_c, h * 16 + (v * 8 + d + 1))
                                A(SS[:, d, :], bank[4 + d][:, 2 * P:3 * P], ACT.Copy).then_inc(s_0, 1)
                    act.wait_ge(e_o, h * 2 + (v + 2))
                    for tt in range(2):
                        last = A(RR[:, tt, :], oo[:, tt, :], ACT.Square, accum_out=rq[:, 2 + tt:3 + tt])
                    last.then_inc(e_ss, 1)
                    act.wait_ge(e_ms, h * 2 + (v + 1))
                    A(rq[:, 4:6], rq[:, 4:6], ACT.Sqrt).then_inc(e_rt, 1)
                    if v:
                        store_out(h, v)
                    tile(3 * v + 2)

            act.sem_inc(e_st, 16)
            for n in range(6):
                tile_act(0, n)
            decays_act(0)
            with act.Fori(0, KH - 1) as h:
                core_act(h, lambda n: tile_act(h + 1, n))
            core_act(KH - 1, lambda n: None, True)
            for q in range(4):
                act.wait_ge(o_back[q], 16)
                A(oH[:, 8 * q:8 * q + 8, :], oraw[:, 8 * q:8 * q + 8, :], ACT.Copy).then_inc(o_hi, 1)
            with act.Fori(0, KC - 1) as i:
                for j in range(2):
                    split(i * 2 + (T_WO2 + j + 2), T_WO2, j + 2, i)
            act.wait_ge(o_ev, 2 * KC + 2)
            squares(2, 1)
            root(2, SEG)
            for n in range(8):
                act.wait_ge(f_T, n + 1)
                A(yout[:, n % 2, (n // 2) * 512:(n // 2 + 1) * 512], bank[4 + n % 4][:], ACT.Copy).then_inc(f_ev, 1)

        @block.vector
        def _(dve):
            V = nc.vector
            link = Linked(dve, dve_done)
            V.memset(ones[:], 1.0).then_inc(ones_ok, 1)
            link(V.memset(cpad[:], 0.0))
            dve.wait_ge(cols_ok, 1)
            dve.wait_ge(act_done, 1)
            link(V.scalar_tensor_tensor(sil[:, 32:64], sil[:, 0:32], 1.0, cols[:, R_C:R_C + 32], ALU.add, ALU.mult))
            V.tensor_scalar(cpad[:, :, 0:2], sil[:, 32:64].rearrange("p (m k) -> p k m", m=2), 0.5, None,
                            ALU.mult).then_inc(cpad_ok, 1)
            for g in range(1, 16, 2):
                s, q = g // 4, g % 4
                dve.wait_ge(tokT, g + 1)
                V.tensor_copy(xT[:, s // 2, 4 * q:4 * q + 4, (s % 2) * P:(s % 2 + 1) * P],
                              bank[g % 4][:].rearrange("p (m t) -> p m t", m=4)).then_inc(tok_dve, 1)
            dve.sem_inc(a_mod, 1)
            with dve.Fori(0, 6) as i:
                dve.wait_ge(a_T, i + 2)
                V.tensor_tensor(mod[:, ds(i * 32, 32)].rearrange("p (j b m) -> p j b m", j=4, b=4),
                                bank[6][:].rearrange("p (b j m) -> p j b m", b=4, j=4)[:, :, :, 0:2],
                                cols[:, ds(i * KC + R_ADA, KC)].rearrange("p (j b) -> p j b", j=4).unsqueeze(3).broadcast_to([P, 4, 4, 2]),
                                ALU.add).then_inc(a_mod, 1)
            dve.wait_ge(a_mod, 7)
            for lay in range(2):
                plus = mod[:, (3 * lay + 1) * 32:(3 * lay + 2) * 32].rearrange("p (k m) -> p k m", m=2)
                link(V.scalar_tensor_tensor(s1[:, lay], plus, 1.0,
                                            cols[:, R_NORM + lay * KC:R_NORM + (lay + 1) * KC].unsqueeze(2).broadcast_to([P, KC, 2]),
                                            ALU.add, ALU.mult))

            def inverse_root(n, cnt=TOK):
                dve.wait_ge(n_sqf, (n + 1) * KC)
                V.tensor_scalar(rstd[:, 0:cnt], bank[0][:, 0:cnt], 1.0 / D, EPS, ALU.mult, ALU.add).then_inc(n_ms, 1)
                dve.wait_ge(n_rt, n + 1)
                link(V.reciprocal(rstd[:, 0:cnt], rstd[:, 0:cnt]))

            def norm(n, lay):
                inverse_root(n)
                with dve.Fori(0, KC // 2) as i:
                    for j in range(2):
                        link.restart()
                        k = i * 2 + j
                        link(V.tensor_tensor(xn[j][:], xT[:, :, ds(k, 1), :].rearrange("p s o t -> p s (o t)"),
                                             rstd[:].rearrange("p (s t) -> p s t", s=2), ALU.mult))
                        for seg in range(2):
                            last = V.tensor_scalar(an[j][:, seg * SEG:(seg + 1) * SEG], xn[j][:, seg, :],
                                                   s1[:, lay].rearrange("p k m -> p (k m)")[:, ds(k * 2 + (1 - seg), 1)],
                                                   mod[:, ds(k * 2 + (96 * lay + 1 - seg), 1)], ALU.mult, ALU.add)
                        last.then_inc(n_a, 1)
                        dve.wait_ge(n_hi, k + (n * KC + 1))
                        V.tensor_tensor(aL[:, ds(k, 1), :].rearrange("p o t -> p (o t)"), an[j][:],
                                        aH[:, ds(k, 1), :].rearrange("p o t -> p (o t)").bitcast(F32),
                                        ALU.subtract).then_inc(n_lo, 1)

            norm(0, 0)
            link.restart()
            dve.sem_inc(i_z, 2)
            with dve.Fori(0, 8) as i:
                for j in range(2):
                    dve.wait_ge(i_tanh, i * 2 + (j + 1))
                    V.scalar_tensor_tensor(zT[:, ds(i * 2 + j, 1), :].rearrange("p o t -> p (o t)"),
                                           tanh_of[j], 1.0, bank[j][:],
                                           ALU.add, ALU.mult).then_inc(i_z, 1)

            def rotate(qk, src, cnt_sem, ok):
                V.tensor_tensor(rt[:, 0, :], src, rsin, ALU.mult).then_inc(dve_done, 1)
                link.n += 1
                link(V.tensor_tensor(rt[:, 1, :], qk, rcos, ALU.mult))
                V.tensor_tensor(qk, rt[:, 0, :], rt[:, 1, :], ALU.add).then_inc(ok, 1)

            for which in range(2):
                dve.wait_ge(l_sum, which + 1)
                V.tensor_scalar(lrt[:, which, :], bank[2 + which][:], 1.0 / LORA, EPS, ALU.mult, ALU.add).then_inc(l_ms, 1)
            dve.wait_ge(kr_sw, 1)
            rotate(krT[:, SEG:TOK], bank[1][0:ROPE, 0:SEG], None, kr_ok)
            dve.wait_ge(l_rt, 1)
            link(V.reciprocal(lrt[:], lrt[:]))
            for k in range(2 * LC):
                V.scalar_tensor_tensor(lat[:, k, :], lat[:, k, :], cols[:, R_QN + k:R_QN + k + 1], lrt[:, k // LC, :],
                                       ALU.mult, ALU.mult).then_inc(l_n, 1)
            for which in range(2):
                dve.wait_ge(l_hi, which + 1)
                V.tensor_tensor(latL[:, which * LC:(which + 1) * LC, :], lat[:, which * LC:(which + 1) * LC, :],
                                latH[:, which * LC:(which + 1) * LC, :].bitcast(F32), ALU.subtract).then_inc(l_lo, 1)

            def head_rope(h, s):
                dve.wait_ge(h_qr, h + 1)
                V.tensor_copy(qrT[s][:], bank[2][0:ROPE, :]).then_inc(h_qrc, 1)
                dve.wait_ge(h_sw, h + 1)
                rotate(qrT[s][:, SEG:TOK], bank[2][0:ROPE, 0:SEG], None, h_rope)

            def softmax(h, s):
                for qt in range(4):
                    n = SEG if qt < 2 else TOK
                    dve.wait_ge(h_s, h * 4 + (qt + 1))
                    link(V.reduce_max(stat[:, 16 * s + qt:16 * s + qt + 1], bank[4 + qt][:, 0:n], AXX))
                    V.tensor_scalar(stat[:, 16 * s + 4 + qt:16 * s + 5 + qt], stat[:, 16 * s + qt:16 * s + qt + 1],
                                    -QK_SCALE, None, ALU.mult).then_inc(h_mx, 1)
                for qt in range(4):
                    n = SEG if qt < 2 else TOK
                    dve.wait_ge(h_e, h * 4 + (qt + 1))
                    link(V.reciprocal(stat[:, 16 * s + 12 + qt:16 * s + 13 + qt], stat[:, 16 * s + 8 + qt:16 * s + 9 + qt]))
                    V.tensor_scalar(pr[qt][:, 0:n], pr[qt][:, 0:n], stat[:, 16 * s + 12 + qt:16 * s + 13 + qt], None,
                                    ALU.mult).then_inc(h_p, 1)

            def finish(h):
                dve.wait_ge(h_pt, h * 3 + 2)
                V.tensor_copy(pT[:, 2:4, :].rearrange("p a b -> p (a b)"), bank[5][:]).then_inc(h_ptd, 1)
                dve.wait_ge(h_o, h + 1)
                z = zT[:, ds(h, 1), :].rearrange("p o t -> p (o t)")
                V.scalar_tensor_tensor(z, bank[7][:], 0.5, z, ALU.mult, ALU.mult).then_inc(h_g, 1)

            dve.sem_inc(h_rope, 1)
            dve.sem_inc(h_ptd, 1)
            dve.sem_inc(h_g, 1)
            head_rope(0, 0)
            with dve.Fori(0, HEADS // 2 - 1) as i:
                for j in range(2):
                    link.restart()
                    softmax(i * 2 + j, j)
                    head_rope(i * 2 + (j + 1), 1 - j)
                    finish(i * 2 + j)
            link.restart()
            softmax(HEADS - 2, 0)
            head_rope(HEADS - 1, 1)
            finish(HEADS - 2)
            softmax(HEADS - 1, 1)
            finish(HEADS - 1)
            for q in range(4):
                dve.wait_ge(g_hi, q + 1)
                V.tensor_tensor(aL[:, 4 * q:4 * q + 4, :], zT[:, 4 * q:4 * q + 4, :],
                                aH[:, 4 * q:4 * q + 4, :].bitcast(F32), ALU.subtract).then_inc(g_lo, 1)

            def residual(m, j, lay, t, segs):
                dve.wait_ge(w_used, t + 3)
                for n, seg in enumerate(segs):
                    xs = xT[:, seg, ds(m, 1), :].rearrange("p o t -> p (o t)")
                    last = V.scalar_tensor_tensor(xs, bank[j][:, n * SEG:(n + 1) * SEG],
                                                  mod[:, ds(m * 2 + ((3 * lay + 2) * 32 + 1 - seg), 1)], xs,
                                                  ALU.mult, ALU.add)
                last.then_inc(o_ev, 1)

            dve.sem_inc(o_ev, 2)
            with dve.Fori(0, KC // 2) as i:
                for j in range(2):
                    residual(i * 2 + j, j, 0, i * 2 + (T_WO + j), (0, 1))
            norm(1, 1)
            dve.wait_ge(b_th, 1)
            V.tensor_scalar(ba[0:64, :], bt[0:64, :], 0.5, 0.5, ALU.mult, ALU.add).then_inc(b_g, 1)
            dve.wait_ge(hb_in, 32)
            link.restart()
            V.tensor_scalar(bt[64:128, :], bank[1][64:128, :], hb[64:128, 0:1], None, ALU.add).then_inc(b_a, 1)
            dve.wait_ge(b_e, 1)
            V.tensor_scalar(bu[64:128, :], bu[64:128, :], 1.0, None, ALU.add).then_inc(b_1, 1)
            dve.wait_ge(b_ea, 1)
            link(V.tensor_scalar(hb[64:128, 3:4], hb[64:128, 2:3], -1.0, None, ALU.mult))
            dve.wait_ge(b_l, 1)
            link(V.scalar_tensor_tensor(bt[64:128, :], bt[64:128, :], 0.0, bu[64:128, :], ALU.max, ALU.add))
            V.tensor_scalar(ba[64:128, :], bt[64:128, :], hb[64:128, 3:4], None, ALU.mult).then_inc(b_g, 1)
            dve.wait_ge(b_ex, 1)
            V.tensor_tensor(sc[:, 3, :, :].rearrange("p c n -> p (c n)"), bank[3][:, SEG:TOK],
                            sc[:, 0, :, :].rearrange("p c n -> p (c n)"), ALU.subtract).then_inc(b_df, 1)
            link(V.tensor_scalar(cols[:, R_CONV:R_CONV + N_CONV], cols[:, R_CONV:R_CONV + N_CONV], 0.5, None, ALU.mult))
            link(V.tensor_scalar(cols[:, R_ON:R_ON + 1], cols[:, R_ON:R_ON + 1], 0.5, None, ALU.mult))
            dve.wait_ge(g_in, 16)
            for q in range(2):
                link(V.memset(pad[q][:], 0.0))
            dve.wait_ge(b_ex, 2)

            def conv(h, n):
                dve.wait_ge(p_pad, h * 4 + (n + 1))
                dve.wait_ge(c_silu, h * 4 + (n + 1))
                row = (h, h + KC, h * 2 + 32, h * 2 + 33)[n]
                segs = slice(1, 2) if n == 0 else slice(0, 2)
                for k in range(5):
                    tap = cols[:, ds(row + (R_CONV + 64 * k), 1)]
                    src = pad[n % 2][:, segs, k:k + SEG]
                    if k == 0:
                        link(V.tensor_scalar(cv[:, segs, :], src, tap, None, ALU.mult))
                    else:
                        last = V.scalar_tensor_tensor(cv[:, segs, :], src, tap, cv[:, segs, :], ALU.mult, ALU.add)
                        if k < 4:
                            link(last)
                last.then_inc(c_conv, 1)

            def silu(h, n):
                dve.wait_ge(c_tanh, h * 4 + (n + 1))
                dst = (qTn, kTn, vTn[0], vTn[1])[n]
                lo = SEG if n == 0 else 0
                V.scalar_tensor_tensor(dst[:], th[:, lo:TOK], 1.0, cv[:].rearrange("p s t -> p (s t)")[:, lo:TOK],
                                       ALU.add, ALU.mult).then_inc(c_silu, 1)

            def zgate(h, v):
                dve.wait_ge(z_tanh, h * 2 + (v + 1))
                V.scalar_tensor_tensor(zsn[:, v, :], th[:, 0:SEG], 1.0, bank[v][:, 0:SEG],
                                       ALU.add, ALU.mult).then_inc(p_z, 1)

            def tile_dve(h, n):
                if n < 4:
                    conv(h, n)
                    silu(h, n)
                else:
                    zgate(h, n - 4)

            def decays_dve(n):
                dve.wait_ge(gb_in, n * 32 + 32)
                for d in range(2):
                    for cc in range(NCH):
                        last = V.tensor_scalar(DT[:, d, cc, :], GB[:, d, cc * P:(cc + 1) * P],
                                               sc[:, 0, cc, ds(n + d * VH, 1)], 0.0, ALU.subtract, ALU.min)
                last.then_inc(d_arg, 1)

            def systems(h, v):
                dve.wait_ge(d_exp, h * 2 + (v + 1))
                dve.wait_ge(k_G, h + 1)
                if v:
                    dve.wait_ge(b_lv, h * 28 + 14)
                for d in range(2):
                    for cc in range(NCH):
                        last = V.scalar_tensor_tensor(AT[:, d, cc, :], Gm[:, d, cc, :], sd[:, 0, cc, d * 2 + v:d * 2 + v + 1],
                                                      DT[:, d, cc, :], ALU.mult, ALU.mult)
                    last.then_inc(d_AT, 1)

            def gate_out(h, v):
                dve.wait_ge(e_T, h * 2 + (v + 1))
                dve.wait_ge(e_st, h * 32 + 16 * (v + 1))
                V.scalar_tensor_tensor(oT[:], bank[7][:, 0:SEG], cols[:, R_ON:R_ON + 1], zs[:, v, :],
                                       ALU.mult, ALU.mult).then_inc(e_cp, 1)

            def core_dve(h, tile, end=False):
                link.restart()
                dve.wait_ge(u_T, h * 3 + 3)
                V.tensor_copy(vt[1][:].rearrange("p c n -> p (c n)"), bank[4][:]).then_inc(k_tokd, 1)
                link(V.tensor_copy(sl[:].rearrange("p k c (d v) -> p (k c) d v", d=2),
                                   sc[:].rearrange("p k c (d n) -> p (k c) d n", d=2)[:, :, :, ds(h * 2, 2)]))
                dve.wait_ge(u_ss, h + 1)
                V.tensor_scalar(nrm[:, 0:6], bank[5][:, 0:6], EPS, None, ALU.add).then_inc(k_ms, 1)
                dve.wait_ge(u_G, h + 1)
                for d in range(2):
                    last = V.tensor_tensor(Gm[:, d], bank[6][:].rearrange("p (c n) -> p c n", c=NCH),
                                           G[:, G_STRICT + d * P:G_STRICT + (d + 1) * P].unsqueeze(1).broadcast_to([P, NCH, P]), ALU.mult)
                last.then_inc(k_G, 1)
                dve.wait_ge(k_rt, h + 1)
                link(V.reciprocal(nrm[:, 6:12], nrm[:, 0:6]))
                dve.wait_ge(u_Q, h + 1)
                for xx in range(2):
                    last = V.scalar_tensor_tensor(Qm[:, :, xx, :], bank[7][:, xx * P:(xx + 1) * P].unsqueeze(1).broadcast_to([P, 2, P]),
                                                  nrm[:, 8 + xx:9 + xx], G[:, G_INCL:G_INCL + 2 * P].rearrange("p (d n) -> p d n", d=2),
                                                  ALU.mult, ALU.mult)
                last.then_inc(k_Q, 1)
                link(V.tensor_scalar(rq[:, 0:2], nrm[:, 10:12], float(DK ** -0.5), None, ALU.mult))
                kinv = nrm[:, 6:10].unsqueeze(2).broadcast_to([P, NCH, 4])
                link(V.tensor_tensor(sd[:, 1], sl[:, 1], kinv, ALU.mult))
                link(V.tensor_tensor(sd[:, 0], sd[:, 1], kinv, ALU.mult))
                link(V.tensor_tensor(sd[:, 2], sl[:, 3], kinv, ALU.mult))
                V.tensor_scalar(sd[:, 3], sl[:, 2], -1.0, None, ALU.mult).then_inc(k_sc, 1)
                dve.wait_ge(k_sc, h + 1)
                systems(h, 0)
                for v in range(2):
                    dve.wait_ge(k_Q, h + 1)
                    V.tensor_tensor(qkd[:], Qm[:], DT[:, :, 2:4, :], ALU.mult).then_inc(d_qk, 1)
                    eye = ident.unsqueeze(1).broadcast_to([P, NCH, P])
                    by_chunk = lambda b: b[:].rearrange("p (c n) -> p c n", c=NCH)
                    for d in range(2):
                        dve.wait_ge(b_lv, h * 28 + (v * 14 + d + 1))
                        V.tensor_tensor(YT[:, d], eye, BT[:, d], ALU.subtract).then_inc(y_up, 1)
                    for d in range(2):
                        dve.wait_ge(x_T, h * 4 + (v * 2 + d + 1))
                        V.tensor_tensor(XF[:, d], eye, by_chunk(bank[4 + d]), ALU.subtract).then_inc(x_up, 1)
                    for lev in range(1, LEVELS):
                        for d in range(2):
                            if lev < LEVELS - 1:
                                dve.wait_ge(x_mm, h * 20 + (v * 10 + (lev - 1) * 2 + d + 1))
                                V.tensor_tensor(XF[:, d], XF[:, d], by_chunk(bank[4 + d]), ALU.subtract).then_inc(x_up, 1)
                            dve.wait_ge(y_mm, h * 24 + (v * 12 + (lev - 1) * 2 + d + 1))
                            V.tensor_tensor(YT[:, d], YT[:, d], by_chunk(bank[2 + d]), ALU.subtract).then_inc(y_up, 1)
                        if v and lev == 1:
                            gate_out(h, 0)
                        if lev in (2, 4):
                            tile(3 * v + lev // 2 - 1)
                    if not (end and v):
                        dve.wait_ge(d_qk, h * 2 + (v + 1))
                        decays_dve(h * 2 + (v + 1))
                    for m in range(1, NCH):
                        for d in range(2):
                            cc = CHUNK_ORDER[d][m]
                            dve.wait_ge(ch_a, h * 12 + (v * 6 + (m - 1) * 2 + d + 1))
                            dve.wait_ge(k_vr, h * 2 + (v + 1))
                            V.scalar_tensor_tensor(RR[:, d, :], bank[4 + d][:, 0:P], sd[:, 3, cc, d * 2 + v:d * 2 + v + 1],
                                                   vt[v][:, cc, :], ALU.mult, ALU.add).then_inc(r_, 1)
                            if m == 2:
                                link(V.tensor_scalar(oo[:, cc - 2, :], bank[2 + d][:, 0:P], sl[:, 2, cc, d * 2 + v:d * 2 + v + 1], None,
                                                     ALU.mult))
                            if m == 3:
                                link(V.scalar_tensor_tensor(oo[:, cc - 2, :], bank[2 + d][:, 0:P], sl[:, 2, cc, d * 2 + v:d * 2 + v + 1],
                                                            oo[:, cc - 2, :], ALU.mult, ALU.add))
                        if m == 1 and not v:
                            systems(h, 1)
                        if m < 3:
                            for d in range(2):
                                cc = CHUNK_ORDER[d][m]
                                dve.wait_ge(ch_c, h * 16 + (v * 8 + m * 2 + d + 1))
                                V.scalar_tensor_tensor(SS[:, d, :], SS[:, d, :], sl[:, 4, cc, d * 2 + v:d * 2 + v + 1],
                                                       bank[4 + d][:, 2 * P:3 * P], ALU.mult, ALU.add).then_inc(s_up, 1)
                    dve.wait_ge(ch_c, h * 16 + (v * 8 + 8))
                    link(V.tensor_tensor(oo[:].rearrange("p a n -> p (a n)"), oo[:].rearrange("p a n -> p (a n)"), bank[6][:, 0:SEG], ALU.add))
                    for tt in range(2):
                        last = V.tensor_scalar(oo[:, tt, :], oo[:, tt, :], rq[:, tt:tt + 1], None, ALU.mult)
                    last.then_inc(e_o, 1)
                    dve.wait_ge(e_ss, h * 2 + (v + 1))
                    V.tensor_scalar(rq[:, 4:6], rq[:, 2:4], 1.0 / P, EPS, ALU.mult, ALU.add).then_inc(e_ms, 1)
                    dve.wait_ge(e_rt, h * 2 + (v + 1))
                    link(V.reciprocal(rq[:, 6:8], rq[:, 4:6]))
                    for tt in range(2):
                        last = V.tensor_scalar(og[:, tt, :], oo[:, tt, :], rq[:, 6 + tt:7 + tt], None, ALU.mult)
                    last.then_inc(e_og, 1)
                    if v:
                        gate_out(h, 1)
                    tile(3 * v + 2)

            dve.sem_inc(p_z, 2)
            dve.sem_inc(c_conv, 2)
            dve.sem_inc(c_silu, 1)
            dve.sem_inc(d_arg, 1)
            dve.sem_inc(e_o, 1)
            for n in range(6):
                tile_dve(0, n)
            decays_dve(0)
            with dve.Fori(0, KH - 1) as h:
                core_dve(h, lambda n: tile_dve(h + 1, n))
            core_dve(KH - 1, lambda n: None, True)
            for q in range(4):
                dve.wait_ge(o_hi, q + 1)
                V.tensor_tensor(oL[:, 8 * q:8 * q + 8, :], oraw[:, 8 * q:8 * q + 8, :],
                                oH[:, 8 * q:8 * q + 8, :].bitcast(F32), ALU.subtract).then_inc(o_lo, 1)
            dve.wait_ge(x_back, 16)
            with dve.Fori(0, KC // 2) as i:
                for j in range(2):
                    residual(i * 2 + j, j, 1, i * 4 + (T_WO2 + 2 * j + 1), (1,))
            link.restart()
            inverse_root(2, SEG)
            for k in range(KC):
                V.scalar_tensor_tensor(yT[:, k, :], xT[:, 1, k, :], cols[:, R_FIN + k:R_FIN + k + 1], rstd[:, 0:SEG],
                                       ALU.mult, ALU.mult).then_inc(f_y, 1)

        @block.gpsimd
        def _(pool):
            GP = nc.gpsimd

            def rest(t, s):
                pool.wait_ge(w_hi, t + 1)
                GP.tensor_tensor(wL[s][:], raw[s][:], wH[s][:].bitcast(F32), ALU.subtract).then_inc(w_lo, 1)

            pool.sem_inc(w_lo, 2)
            with pool.Fori(0, T_GDN // 2 + 3) as i:
                for j in range(2):
                    rest(i * 2 + j, j)

            def core_pool(h, stream):
                for n in range(2):
                    rest(h * 6 + (T_GDN + 6 + n), n)
                pool.wait_ge(k_sc, h + 1)
                pool.wait_ge(k_tok, h * 2 + 2)
                for v in range(2):
                    bcast = lambda col: G[:, col:col + P].unsqueeze(1).broadcast_to([P, NCH, P])
                    for d in range(2):
                        pool.wait_ge(d_AT, h * 4 + (v * 2 + d + 1))
                        if v:
                            pool.wait_ge(x_p, h * 24 + (10 + d + 1))
                        GP.tensor_tensor(BT[:, d], AT[:, d], bcast(G_M), ALU.mult).then_inc(b_lv, 1)
                    if stream and v:
                        rest(h * 6 + (T_GDN + 10), 0)
                    for lev in range(1, LEVELS):
                        for d in range(2):
                            if lev == 1:
                                pool.wait_ge(x_T, h * 4 + (v * 2 + d + 1))
                                pool.wait_ge(y_up, h * 28 + (v * 14 + d + 1))
                            else:
                                pool.wait_ge(x_p, h * 24 + (v * 12 + (lev - 2) * 2 + d + 1))
                            GP.tensor_tensor(BT[:, d], AT[:, d], bcast(G_M + lev * P), ALU.mult).then_inc(b_lv, 1)
                        if lev <= 2:
                            for m in range(3):
                                cc = CHUNK_ORDER[lev - 1][m]
                                last = GP.tensor_scalar(kdec[:, lev - 1, m, :], ktok[:, cc, :],
                                                        sd[:, 2, cc, (lev - 1) * 2 + v:(lev - 1) * 2 + v + 1], None, ALU.mult)
                            if lev == 2:
                                last.then_inc(kd_, 1)
                        if stream and (v, lev) in ((0, 3), (0, 5), (1, 3)):
                            n = {(0, 3): 2, (0, 5): 3, (1, 3): 5}[v, lev]
                            rest(h * 6 + (T_GDN + 6 + n), n % 2)

            with pool.Fori(0, KH - 1) as h:
                core_pool(h, True)
            core_pool(KH - 1, False)
            with pool.Fori(0, KC - 1) as i:
                for j in range(2):
                    rest(i * 2 + (T_WO2 + j + 2), j)


_INS = ['x', 'c', 'ctx', 'c_ctx', 'ada_w', 'ada_b', 'norm_w', 'mla_w_in', 'mla_q_norm', 'mla_w_uq', 'mla_kv_norm',
        'mla_w_ukv', 'mla_w_o', 'gdn_w_in', 'gdn_conv_w', 'gdn_a_log', 'gdn_dt_bias', 'gdn_o_norm', 'gdn_w_o',
        'final_norm']


def kernel(**inputs):
    import concourse.bacc as _bacc
    from concourse.bass_utils import run_bass_kernel_spmd as _run

    nc = _bacc.Bacc("TRN2", target_bir_lowering=False, num_devices=1)
    arrays, args = {}, []
    for name in _INS:
        a = np.ascontiguousarray(inputs[name])
        arrays[f"in_{name}"] = a
        args.append(nc.dram_tensor(f"in_{name}", a.shape, mybir.dt.from_np(a.dtype), kind="ExternalInput").ap())
    arrays["shape_constants"] = shape_constants()
    args.append(nc.dram_tensor("shape_constants", (P, C_ALL), F32, kind="ExternalInput").ap())
    args.append(nc.dram_tensor("out_0", (1, SEG, D), F32, kind="ExternalOutput").ap())
    args.append(nc.dram_tensor("gated_heads", (VH, P, SEG), F32).ap())
    args.append(nc.dram_tensor("decay_sums", (2 * VH, TOK), F32).ap())
    args.append(nc.dram_tensor("residual", (P, KC * SEG), F32).ap())
    build(nc, *args)
    r = _run(nc, [arrays], core_ids=[0])
    return r.results[0]["out_0"]
```
